# Optimizing a Trainium2 kernel written in Bass

```python
import math
import jax, jax.numpy as jnp
from jax import lax
import numpy as np

D_MODEL = 1024
BATCH = 1
SEQ = 256
DEPTH = 2

N_HEADS = 16
HEAD_DIM = D_MODEL // N_HEADS
N_A_LAYERS = DEPTH // 2
N_B_LAYERS = DEPTH - N_A_LAYERS
Q_BLOCK = 128
DILATED_GROUPS = ((128, 1), (512, 4), (2048, 16))
N_GROUPS = len(DILATED_GROUPS)
NUM_BUCKETS = 32
MAX_DISTANCE = 2048
D_FF = -(-8 * D_MODEL // (3 * 256)) * 256
RMS_EPS = 1e-6
NEG_INF = -1e30

kernel_name = "yoco_stickbreak_dilated_hybrid"

def rms_norm(x, g):
    xf = x.astype(jnp.float32)
    y = xf * lax.rsqrt(jnp.mean(xf * xf, axis=-1, keepdims=True) + RMS_EPS)
    return (y * g.astype(jnp.float32)).astype(x.dtype)

def swiglu(x, w_gate_up, w_down):
    gate, up = jnp.split(x @ w_gate_up, 2, axis=-1)
    return (jax.nn.silu(gate) * up) @ w_down

def stick_breaking_attention(q, k, v):
    b, h, s, dh = q.shape
    nb = s // Q_BLOCK
    scale = dh ** -0.5
    kf = k.astype(jnp.float32)
    vf = v.astype(jnp.float32)
    qb = q.reshape(b, h, nb, Q_BLOCK, dh).transpose(2, 0, 1, 3, 4)
    key_pos = jnp.arange(s)

    def one_block(args):
        q_blk, j = args
        z = jnp.einsum('bhqd,bhkd->bhqk', q_blk.astype(jnp.float32), kf) * scale
        q_pos = j * Q_BLOCK + jnp.arange(Q_BLOCK)
        strict = key_pos[None, :] < q_pos[:, None]
        log_stay = jnp.where(strict, jax.nn.log_sigmoid(-z), 0.0)
        after = jnp.concatenate([log_stay[..., 1:], jnp.zeros_like(log_stay[..., :1])], axis=-1)
        log_a = jax.nn.log_sigmoid(z) + lax.cumsum(after, axis=3, reverse=True)
        a = jnp.where(strict, jnp.exp(log_a), 0.0)
        return jnp.einsum('bhqk,bhkd->bhqd', a, vf)

    out = lax.map(one_block, (qb, jnp.arange(nb)))
    return out.transpose(1, 2, 0, 3, 4).reshape(b, h, s, dh).astype(q.dtype)

def mixer_a(xn, w_qkv, w_o):
    b, s, _ = xn.shape
    qkv = (xn @ w_qkv).reshape(b, s, 3, N_HEADS, HEAD_DIM)
    q = qkv[:, :, 0].transpose(0, 2, 1, 3)
    k = qkv[:, :, 1].transpose(0, 2, 1, 3)
    v = qkv[:, :, 2].transpose(0, 2, 1, 3)
    o = stick_breaking_attention(q, k, v)
    return o.transpose(0, 2, 1, 3).reshape(b, s, D_MODEL) @ w_o

def to_strided_blocks(t, dilation):
    b, s, h, dh = t.shape
    L = s // dilation
    nb = -(-L // Q_BLOCK)
    t = t.reshape(b, L, dilation, h, dh).transpose(0, 2, 3, 1, 4)
    t = jnp.pad(t, ((0, 0), (0, 0), (0, 0), (0, nb * Q_BLOCK - L), (0, 0)))
    return t.reshape(b, dilation, h, nb, Q_BLOCK, dh)

def banded_keys(kb):
    prev = jnp.concatenate([jnp.zeros_like(kb[:, :, :, :1]), kb[:, :, :, :-1]], axis=3)
    return jnp.concatenate([prev, kb], axis=4)

def from_strided_blocks(t, s):
    b, d, h, nb, blk = t.shape[:5]
    rest = t.shape[5:]
    L = s // d
    t = t.reshape((b, d, h, nb * blk) + rest)[:, :, :, :L]
    t = jnp.moveaxis(t, 3, 1)
    return t.reshape((b, s, h) + rest)

def relative_bucket(distance):
    max_exact = NUM_BUCKETS // 2
    n = jnp.maximum(distance, 0)
    large = max_exact + (jnp.log(jnp.maximum(n, 1).astype(jnp.float32) / max_exact)
                         / math.log(MAX_DISTANCE / max_exact)
                         * (NUM_BUCKETS - max_exact)).astype(jnp.int32)
    large = jnp.minimum(large, NUM_BUCKETS - 1)
    return jnp.where(n < max_exact, n, large)

def dilated_group_attention(qb, kk, vv, rel_bias, window, dilation):
    nb = qb.shape[3]
    w_sub = window // dilation
    scale = HEAD_DIM ** -0.5
    i = jnp.arange(Q_BLOCK)[:, None]
    m = jnp.arange(2 * Q_BLOCK)[None, :]
    rel = Q_BLOCK + i - m
    band = (rel >= 0) & (rel <= w_sub)
    blk = jnp.arange(nb)[:, None, None]
    valid = band[None] & (blk * Q_BLOCK - Q_BLOCK + m[None] >= 0)
    bias = rel_bias[relative_bucket(rel * dilation)]
    bias = jnp.transpose(bias, (2, 0, 1))[:, None].astype(jnp.float32)
    s = jnp.einsum('brhnqd,brhnkd->brhnqk', qb.astype(jnp.float32), kk.astype(jnp.float32)) * scale + bias
    s = jnp.where(valid, s, NEG_INF)
    lse = jax.nn.logsumexp(s, axis=-1)
    p = jnp.exp(s - lse[..., None])
    o = jnp.einsum('brhnqk,brhnkd->brhnqd', p, vv.astype(jnp.float32))
    return o, lse

def shared_kv_from(x, g_kv, w_kv):
    b, s, _ = x.shape
    kv = (rms_norm(x, g_kv) @ w_kv).reshape(b, s, N_GROUPS, 2, N_HEADS, HEAD_DIM)
    out = []
    for g, (_, dilation) in enumerate(DILATED_GROUPS):
        out.append(banded_keys(to_strided_blocks(kv[:, :, g, 0], dilation)))
        out.append(banded_keys(to_strided_blocks(kv[:, :, g, 1], dilation)))
    return out

def mixer_b(xn, shared_kv, w_q, w_o, rel_bias):
    b, s, _ = xn.shape
    q = (xn @ w_q).reshape(b, s, N_GROUPS, N_HEADS, HEAD_DIM)
    outs, lses = [], []
    for g, (window, dilation) in enumerate(DILATED_GROUPS):
        qb = to_strided_blocks(q[:, :, g], dilation)
        o, lse = dilated_group_attention(qb, shared_kv[2 * g], shared_kv[2 * g + 1], rel_bias, window, dilation)
        outs.append(from_strided_blocks(o, s))
        lses.append(from_strided_blocks(lse, s))
    o = jnp.stack(outs, axis=0)
    lse = jnp.stack(lses, axis=0)
    wts = jax.nn.softmax(lse, axis=0)
    o = jnp.sum(wts[..., None] * o, axis=0)
    return o.reshape(b, s, D_MODEL).astype(xn.dtype) @ w_o

def setup_inputs(seed: int = 0) -> dict:
    key = jax.random.key(seed)
    ks = jax.random.split(key, 12)
    f32 = jnp.float32
    d = D_MODEL
    x = jax.random.normal(ks[0], (BATCH, SEQ, d), f32)
    norm_gains = 1.0 + 0.1 * jax.random.normal(ks[1], (DEPTH, 4, d), f32)
    w_qkv_a = jax.random.normal(ks[2], (N_A_LAYERS, d, 3 * d), f32) * d ** -0.5
    w_o_a = jax.random.normal(ks[3], (N_A_LAYERS, d, d), f32) * d ** -0.5
    g_kv = 1.0 + 0.1 * jax.random.normal(ks[4], (d,), f32)
    w_kv_b = jax.random.normal(ks[5], (d, N_GROUPS * 2 * d), f32) * d ** -0.5
    w_q_b = jax.random.normal(ks[6], (N_B_LAYERS, d, N_GROUPS * d), f32) * d ** -0.5
    w_o_b = jax.random.normal(ks[7], (N_B_LAYERS, d, d), f32) * d ** -0.5
    rel_bias = 0.5 * jax.random.normal(ks[8], (NUM_BUCKETS, N_HEADS), f32)
    w_gate_up = jax.random.normal(ks[9], (DEPTH, d, 2 * D_FF), f32) * d ** -0.5
    w_down = jax.random.normal(ks[10], (DEPTH, D_FF, d), f32) * D_FF ** -0.5
    return {"x": x, "norm_gains": norm_gains, "w_qkv_a": w_qkv_a, "w_o_a": w_o_a,
            "g_kv": g_kv, "w_kv_b": w_kv_b, "w_q_b": w_q_b, "w_o_b": w_o_b,
            "rel_bias": rel_bias, "w_gate_up": w_gate_up, "w_down": w_down}

def reference(x, norm_gains, w_qkv_a, w_o_a, g_kv, w_kv_b, w_q_b, w_o_b, rel_bias, w_gate_up, w_down):
    shared_kv = None
    for layer in range(DEPTH):
        g = norm_gains[layer]
        h = rms_norm(x, g[0])
        if layer < N_A_LAYERS:
            h = mixer_a(h, w_qkv_a[layer], w_o_a[layer])
        else:
            if layer == N_A_LAYERS:
                shared_kv = shared_kv_from(x, g_kv, w_kv_b)
            j = layer - N_A_LAYERS
            h = mixer_b(h, shared_kv, w_q_b[j], w_o_b[j], rel_bias)
        x = x + rms_norm(h, g[1])
        h = swiglu(rms_norm(x, g[2]), w_gate_up[layer], w_down[layer])
        x = x + rms_norm(h, g[3])
    return x


_drawn_inputs = setup_inputs


def setup_inputs(seed=0):
    import zlib

    import numpy as np

    out = dict(_drawn_inputs(seed))
    spreads = {}
    factors = {}
    for name, (base, spread) in spreads.items():
        noise = np.random.default_rng([zlib.crc32(name.encode()), seed]).standard_normal(out[name].shape)
        drawn = base * np.exp(spread * noise) if base else spread * noise
        out[name] = __import__('jax').numpy.asarray(drawn.astype(out[name].dtype))
    for name, factor in factors.items():
        out[name] = (out[name] * factor).astype(out[name].dtype)
    return out
```

```python
import math

import numpy as np
import concourse.bass as bass
from concourse import mybir
from contextlib import ExitStack

D = 1024
SEQ = 256
P = 128
NT = SEQ // P
KT = D // P
NH = 16
DH = D // NH
PAIRS = NH // 2
FF = 2816
FC = 256
STEPS = FF // FC
GROUPS = ((128, 1), (512, 4), (2048, 16))
NG = len(GROUPS)
BUCKETS = 32
MAX_DISTANCE = 2048
EPS = 1e-6
SCALE = DH ** -0.5
OUTSIDE = -1e30
LOWEST = -3e38

HALF = D // 2
UNIT = 2048
RAW = 3
CUT = 6
WORK = 6784

A0 = 0
WOA0 = A0 + 3 * PAIRS
FA0 = WOA0 + 4
B0 = FA0 + 3 * STEPS
WOB0 = B0 + 6 * PAIRS
FB0 = WOB0 + 4
UNITS = FB0 + 3 * STEPS


def shape_constants():
    i = np.arange(P)
    eye = np.eye(P, dtype=np.float32)
    later = (i[:, None] > i[None, :]).astype(np.float32)
    strict = (i[:, None] < i[None, :]).astype(np.float32)
    square = np.stack([eye, later, strict, np.ones((P, P), np.float32)], 1)
    dist = P + i[:, None] - np.arange(2 * P)[None, :]
    mask = np.zeros((P, NG, 2 * P), np.float32)
    for g, (window, dilation) in enumerate(GROUPS):
        seen = (dist >= 0) & (dist % dilation == 0) & (dist // dilation <= window // dilation)
        mask[:, g] = np.where(seen, 0.0, OUTSIDE)
    n = np.maximum(2 * P - 1 - np.arange(3 * P), 0)
    exact = BUCKETS // 2
    large = exact + (np.log(np.maximum(n, 1).astype(np.float32) / exact)
                     / math.log(MAX_DISTANCE / exact) * (BUCKETS - exact)).astype(np.int32)
    bucket = np.where(n < exact, n, np.minimum(large, BUCKETS - 1))
    select = (bucket[None, :] == np.arange(BUCKETS)[:, None]).astype(np.float32)
    return {"square": square, "mask": mask, "select": select}


def build(nc, x, norm_gains, w_qkv_a, w_o_a, g_kv, w_kv_b, w_q_b, w_o_b, rel_bias, w_gate_up, w_down,
          square, mask, select, out):
    F32, F32R, BF16 = mybir.dt.float32, mybir.dt.float32r, mybir.dt.bfloat16
    ACT, ALU = mybir.ActivationFunctionType, mybir.AluOpType
    ds = bass.ds

    x_dram = x[0].rearrange("(t p) d -> t p d", p=P)
    out_dram = out[0].rearrange("(t p) d -> t p d", p=P)
    qkv_dram = w_qkv_a[0].rearrange("(k p) (c n) -> p c k n", p=P, c=3)
    q_dram = w_q_b[0].rearrange("(k p) (g n) -> p k g n", p=P, g=NG)
    kv_dram = w_kv_b.rearrange("(k p) (g c n) -> p c k g n", p=P, g=NG, c=2)
    wo_dram = [w[0].rearrange("(k p) n -> p k n", p=P) for w in (w_o_a, w_o_b)]
    up_dram = [w_gate_up[l].rearrange("(k p) (c n) -> p k c n", p=P, c=2) for l in range(2)]
    down_dram = [w_down[l].rearrange("(k p) n -> p k n", p=P) for l in range(2)]
    gain_rows = norm_gains.rearrange("l g (k p) -> (l g k) p", p=P)
    bias_rows = nc.dram_tensor("bias_rows", [NH, 3 * P], F32, kind="Internal").ap()

    with ExitStack() as ctx:
        def sb(name, shape, dt=F32):
            return ctx.enter_context(nc.sbuf_tensor(name, shape, dt))

        def sem(name):
            return ctx.enter_context(nc.semaphore(name))

        bands = nc.dram_tensor("bands", [NH, P, 2 * P], F32, kind="Internal").ap()
        ROWS_TO_BANDS = bass.AP(bias_rows.tensor, bias_rows.offset + (P - 1), [[3 * P, NH], [-1, P], [1, 2 * P]])

        raw = sb("raw", [P, RAW, UNIT])
        w_hi = sb("w_hi", [P, CUT, UNIT], F32R)
        w_lo = sb("w_lo", [P, CUT, UNIT], F32R)
        xt = sb("xt", [P, 2, KT, SEQ], F32R)
        xkv = sb("xkv", [P, 2, KT, SEQ], F32R)
        ot = sb("ot", [P, 2, KT, SEQ], F32R)
        xn = sb("xn", [P, NT, D])
        eye = sb("eye", [P, P])
        ones = sb("ones", [P, P])
        gains = sb("gains", [P, 9 * KT])
        mask_b = sb("mask_b", [P, NG, 2 * P], BF16)
        rows = sb("rows", [P, SEQ])
        ob = sb("ob", [P, NT, P])
        stat = sb("stat", [P, 48])
        expo = sb("expo", [P, 1])
        work = sb("work", [P, WORK])

        end = [0]

        def carve(n, at=None):
            end[0] = (end[0] if at is None else at) + n
            assert end[0] <= WORK
            return work[:, end[0] - n:end[0]]

        gain_in = carve(P, 0)
        select_in = carve(3 * P)
        rel_in = carve(NH)
        mask_in = carve(NG * 2 * P).rearrange("p (g s) -> p g s", g=NG)
        bias_out = carve(3 * P)
        WA = 3 * P
        qa = carve(SEQ)
        ka = carve(SEQ)
        va_t = carve(SEQ)
        va = carve(SEQ)
        later = carve(P)
        strict = carve(P)
        at = end[0]
        ell, spl, arg, wts = (carve(2 * WA).rearrange("p (h n) -> p h n", h=2) for _ in range(4))
        in_xkv = [xkv[:, n, :, :].rearrange("p k s -> p (k s)") for n in range(2)]
        spl_cut = [v[:, 0:2 * WA].rearrange("p (h n) -> p h n", h=2) for v in in_xkv]
        later_r, ones_r = (v[:, 2 * WA:2 * WA + P] for v in in_xkv)
        squares_a = carve(D, at)
        post = carve(D, 0)
        delta = carve(D)
        squares = carve(D)
        silu = carve(NT * FC).rearrange("p (t n) -> p t n", t=NT)
        hid = carve(NT * FC).rearrange("p (t n) -> p t n", t=NT)
        qb = carve(2 * NG * SEQ, 0).rearrange("p (b g n) -> p b g n", b=2, g=NG)
        kb = carve(2 * NG * SEQ).rearrange("p (b g n) -> p b g n", b=2, g=NG)
        vb = carve(NT * NG * P).rearrange("p (t n) -> p t n", t=NT)
        W0, W1 = NG * P, NG * 2 * P
        prob = carve(W0 + W1)
        bias = carve(2 * W1).rearrange("p (b g s) -> p b g s", b=2, g=NG)
        band = carve(2 * P)

        def column(first):
            return lambda n, t: stat[:, first + NT * n + t:first + NT * n + t + 1]

        x_sq, x_rs, h_sq0, h_sq1, h_rs = (column(8 * c) for c in range(5))
        h_sq = (h_sq0, h_sq1)
        peak, npeak, total, inv = (stat[:, 40 + 2 * c:42 + 2 * c] for c in range(4))

        ps = ctx.enter_context(nc.psum_tensor("ps", [P, 8 * 512], F32))

        def bank(b, lo=0, n=512):
            return ps[:, 512 * b + lo:512 * b + lo + n]

        def two_heads(b, n):
            return bank(b, 0, 2 * n).rearrange("p (h n) -> p h n", h=2)

        def banks(b, m, n):
            return ps[:, 512 * b:512 * (b + m)].rearrange("p (m n) -> p m n", m=m)[:, :, 0:n]

        landed = [sem(f"landed{r}") for r in range(RAW)]
        hi_made, lo_made = sem("hi_made"), sem("lo_made")
        w_used = sem("w_used")
        x_in = [sem(f"x_in{t}") for t in range(NT)]
        eye_in, ones_in, later_in, strict_in, gain_in_s, bias_in, mask_in_s = (sem(n) for n in (
            "eye_in", "ones_in", "later_in", "strict_in", "gain_in", "bias_in", "mask_in"))
        post_in, band_in, bias_stored, out_stored = (sem(n) for n in (
            "post_in", "band_in", "bias_stored", "out_stored"))
        zeros_made = sem("zeros_made")
        gain_done, gain_made, bias_done, bias_out_made, mask_made, expo_made = (sem(n) for n in (
            "gain_done", "gain_made", "bias_done", "bias_out_made", "mask_made", "expo_made"))
        x_made, delta_made, xsq_made, hsq_made, xrs_made, hrs_made, mean_made = (sem(n) for n in (
            "x_made", "delta_made", "xsq_made", "hsq_made", "xrs_made", "hrs_made", "mean_made"))
        xt_done, xt_hi, xt_made, diag_made, rows_done, rows_made = (sem(n) for n in (
            "xt_done", "xt_hi", "xt_made", "diag_made", "rows_done", "rows_made"))
        acc_done = sem("acc_done")
        ot_hi, ot_made = sem("ot_hi"), sem("ot_made")
        z_done, vt_done, r_done, pva_done = (sem(n) for n in ("z_done", "vt_done", "r_done", "pva_done"))
        qka_made, vat_made, va_made, abs_made, exp_made, ell_made = (sem(n) for n in (
            "qka_made", "vat_made", "va_made", "abs_made", "exp_made", "ell_made"))
        spl_made, spl_masked, spl_hi, spl_cut_made, arg_made, stay_made, wts_made, wts_masked = (sem(n) for n in (
            "spl_made", "spl_masked", "spl_hi", "spl_cut_made", "arg_made", "stay_made", "wts_made", "wts_masked"))
        exact_made = sem("exact_made")
        job_done, qkb_made, vb_made, obt_done = (sem(n) for n in ("job_done", "qkb_made", "vb_made", "obt_done"))
        bias_made, s_done, sum_made, peak_made, prob_made, inv_made, pt_done, pt_made, pvb_done, ob_made = (
            sem(n) for n in ("bias_made", "s_done", "sum_made", "peak_made", "prob_made", "inv_made",
                             "pt_done", "pt_made", "pvb_done", "ob_made"))
        up0_done, silu_made, hid_made, ht_done, ht_hi, ht_made = (sem(n) for n in (
            "up0_done", "silu_made", "hid_made", "ht_done", "ht_hi", "ht_made"))

        block = ctx.enter_context(nc.Block())

        def size(s):
            return KT * P if s < WOA0 else 4 * NG * P if B0 <= s < WOB0 else UNIT

        def parts(s):
            if B0 <= s < WOB0:
                return NG
            first = FA0 if s < B0 else FB0
            n = s - first
            is_down = n >= 2 and (n - 2) % 3 == 2 or n == 3 * STEPS - 1
            return 1 if n < 0 or is_down else 2

        def arrived(s):
            return 16 * sum(parts(u) for u in range(s % RAW, s + 1, RAW))

        def hidden_at(i):
            return slice(2, 4) if i == STEPS - 1 else slice(0, 2)

        @block.sync
        def _(sp):
            def load(s, j, shape, src):
                dst = raw[:, s % RAW, 0:size(s)]
                if s >= RAW:
                    sp.wait_ge(lo_made, j * 6 + (s - RAW + 1))
                d, n = shape(dst), parts(s)
                for c in range(n):
                    sp.dma_start(d[:, :, c, :] if n > 1 else d, src[:, :, c, :] if n > 1 else src
                                 ).then_inc(landed[s % RAW], 16)

            def pair_a(p, j):
                for c in range(3):
                    load(A0 + 3 * p + c, j, lambda r: r.rearrange("p (k n) -> p k n", k=KT),
                         qkv_dram[:, c, :, ds(j * (2 * P) + p * P, P)])

            def pair_b(p, j):
                for n, c in enumerate((2, 0, 1) if p == 0 else (0, 1, 2)):
                    for half in range(2):
                        k4, cols = slice(4 * half, 4 * half + 4), ds(j * P + p * P, P)
                        load(B0 + 6 * p + 2 * n + half, j,
                             lambda r: r.rearrange("p (k g n) -> p k g n", k=4, g=NG),
                             q_dram[:, k4, :, cols] if c == 0 else kv_dram[:, c - 1, k4, :, cols])

            def gate_up(l, s, i, j):
                for half in range(2):
                    load(s + half, j, lambda r: r.rearrange("p (k c n) -> p k c n", k=4, c=2),
                         up_dram[l][:, 4 * half:4 * half + 4, :, ds(j * (2 * FC) + i * FC, FC)])

            def two_rows(s, j, src):
                load(s, j, lambda r: r.rearrange("p (k n) -> p k n", k=2), src)

            def swiglu(l, s0):
                gate_up(l, s0, 0, 0)
                with sp.Fori(0, (STEPS - 1) // 2) as j:
                    for i in (1, 2):
                        gate_up(l, s0 + 3 * i - 1, i, j)
                        two_rows(s0 + 3 * i + 1, j, down_dram[l][:, ds(j * 4 + 2 * (i - 1), 2), :])
                two_rows(s0 + 3 * STEPS - 1, 0, down_dram[l][:, 2 * STEPS - 2:2 * STEPS, :])

            sp.dma_start(eye[:, :], square[:, 0, :]).then_inc(eye_in, 16)
            for t in range(NT):
                sp.dma_start(xn[:, t, :], x_dram[t]).then_inc(x_in[t], 16)
            pair_a(0, 0)
            sp.dma_start(ones[:, :], square[:, 3, :]).then_inc(ones_in, 16)
            sp.dma_start(select_in[0:BUCKETS, :], select).then_inc(bias_in, 16)
            sp.dma_start(rel_in[0:BUCKETS, :], rel_bias).then_inc(bias_in, 16)
            sp.dma_start(later, square[:, 1, :]).then_inc(later_in, 16)
            sp.dma_start(strict, square[:, 2, :]).then_inc(strict_in, 16)
            pair_a(1, 0)
            sp.dma_start(mask_in, mask).then_inc(mask_in_s, 16)
            with sp.Fori(0, 3) as j:
                pair_a(2, j)
                pair_a(3, j)
            for u in range(4):
                two_rows(WOA0 + u, 0, wo_dram[0][:, 2 * u:2 * u + 2, :])
            swiglu(0, FA0)
            pair_b(0, 0)
            with sp.Fori(0, PAIRS - 1) as j:
                pair_b(1, j)
            for u in range(4):
                two_rows(WOB0 + u, 0, wo_dram[1][:, 2 * u:2 * u + 2, :])
            swiglu(1, FB0)
            for t in range(NT):
                for half in range(2):
                    sp.wait_ge(x_made, 6 * NT + 2 * t + half + 1)
                    cols = slice(HALF * half, HALF * half + HALF)
                    sp.dma_start(out_dram[t][:, cols], xn[:, t, cols]).then_inc(out_stored, 16)
            sp.wait_ge(out_stored, 32 * NT)

        @block.gpsimd
        def _(pool):
            means = [0]

            def root(dst, src, made, more=0.0):
                pool.tensor_scalar(dst, src, more, EPS, ALU.add, ALU.add).then_inc(mean_made, 1)
                means[0] += 1
                pool.wait_ge(mean_made, means[0])
                pool.tensor_tensor(dst, dst, expo[:, :], ALU.pow).then_inc(made, 1)

            def stats(b):
                def output(t):
                    pool.wait_ge(hsq_made, 2 * (NT * b + t) + 2)
                    root(h_rs(b, t), h_sq[0](b, t), hrs_made, h_sq[1](b, t))

                def stream(t):
                    pool.wait_ge(xsq_made, NT * (b + 1) + t + 1)
                    root(x_rs(b + 1, t), x_sq(b + 1, t), xrs_made)

                for part in (output, stream) if b < 3 else (output,):
                    for t in range(NT):
                        part(t)

            def load_post(row):
                pool.dma_start(post, row.broadcast_to([P, D])).then_inc(post_in, 16)

            pool.memset(expo[:, :], -0.5).then_inc(expo_made, 1)
            pool.wait_ge(expo_made, 1)
            for t in range(NT):
                pool.wait_ge(xsq_made, t + 1)
                root(x_rs(0, t), x_sq(0, t), xrs_made)
            pool.wait_ge(bias_out_made, 1)
            pool.dma_start(bias_rows, bias_out[0:NH, :]).then_inc(bias_stored, 16)
            pool.wait_ge(bias_stored, 16)
            pool.wait_ge(mask_made, 1)
            pool.wait_ge(pva_done, PAIRS)
            load_post(norm_gains[0, 1:2, :])
            stats(0)
            pool.wait_ge(x_made, 2 * NT)
            load_post(norm_gains[0, 3:4, :])
            pool.dma_start(bands, ROWS_TO_BANDS).then_inc(bias_stored, 16)
            pool.wait_ge(bias_stored, 32)
            stats(1)
            pool.wait_ge(x_made, 4 * NT)

            def head_bias(b, h):
                static = isinstance(h, int)
                if not static or h >= 1:
                    pool.wait_ge(bias_made, h)
                pool.dma_start(band, bands[ds(h, 1)].rearrange("h t s -> (h t) s")).then_inc(band_in, 16)
                pool.wait_ge(band_in, h * 16 + 16)
                if not static or h >= 2:
                    pool.wait_ge(sum_made, h - 1)
                pool.tensor_tensor(bias[:, b], mask_b[:, :, :],
                                   band.rearrange("p (g s) -> p g s", g=1).broadcast_to([P, NG, 2 * P]),
                                   ALU.add).then_inc(bias_made, 1)

            head_bias(0, 0)
            head_bias(1, 1)
            with pool.Fori(0, PAIRS - 1) as j:
                head_bias(0, j * 2 + 2)
                head_bias(1, j * 2 + 3)
            pool.wait_ge(pvb_done, NH)
            load_post(norm_gains[1, 1:2, :])
            stats(2)
            pool.wait_ge(x_made, 6 * NT)
            load_post(norm_gains[1, 3:4, :])
            stats(3)

        @block.scalar
        def _(act):
            def hi(s, j=0):
                act.wait_ge(landed[s % RAW], j * (16 * (parts(s) + parts(s + RAW))) + arrived(s))
                if s >= CUT:
                    act.wait_ge(w_used, j * 6 + (s - CUT + 1))
                act.activation(w_hi[:, s % CUT, 0:size(s)], raw[:, s % RAW, 0:size(s)], ACT.Copy
                               ).then_inc(hi_made, 1)

            def square_h(b, t, last):
                for half in range(2):
                    if t == 0:
                        act.wait_ge(acc_done, 2 * b + 1)
                        if b >= 1:
                            act.wait_ge(xsq_made, NT * b + NT)
                    else:
                        act.wait_ge(*((acc_done, 2 * b + 2) if half == 0 else (w_used, last + 1)))
                        act.wait_ge(hsq_made, 2 * NT * b + 1 + half)
                    cols = slice(HALF * half, HALF * half + HALF)
                    act.activation(squares[:, cols], ps[:, D * t + HALF * half:D * t + HALF * half + HALF], ACT.Square,
                                   scale=D ** -0.5, accum_out=h_sq[half](b, t)).then_inc(hsq_made, 1)

            def square_x(b, t):
                act.wait_ge(*((hsq_made, 2 * NT * (b + 1)) if t == 0 else (xsq_made, NT * (b + 1) + 1)))
                act.wait_ge(x_made, 2 * (NT * b + t) + 2)
                act.activation(squares, xn[:, t, :], ACT.Square, scale=D ** -0.5, accum_out=x_sq(b + 1, t)
                               ).then_inc(xsq_made, 1)

            def cut_x(n, t, first_bank, dst, gain, after=None):
                for k in range(KT):
                    if k % 4 == 0 and after is not None:
                        act.wait_ge(xt_made, after + k + 4)
                    if k % 4 == 0:
                        act.wait_ge(xt_done, 4 * n + 2 * t + k // 4 + 1)
                    act.activation(dst[:, 0, k, P * t:P * t + P], bank(first_bank + k // 4, P * (k % 4), P), ACT.Copy,
                                   scale=gains[:, KT * gain + k:KT * gain + k + 1]).then_inc(xt_hi, 1)

            def boundary(b, last, gain):
                act.preload_act_table(ACT.Silu)
                square_h(b, 0, last)
                hi(last + 3)
                cut_x(b + 1, 0, 6, xt, gain)
                square_h(b, 1, last)
                square_x(b, 0)
                hi(last + 4)
                cut_x(b + 1, 1, 0, xt, gain)
                square_x(b, 1)

            def attend_a(a, j, between):
                if a >= 1:
                    act.wait_ge(arg_made, j * 2 + a)
                act.wait_ge(z_done, j * 2 + a + 1)
                act.activation(ell, banks(3, 2, WA), ACT.Abs).then_inc(abs_made, 1)
                act.wait_ge(abs_made, j * 2 + a + 1)
                act.activation(ell, ell, ACT.Exp, scale=-1.0).then_inc(exp_made, 1)
                act.wait_ge(exp_made, j * 2 + a + 1)
                act.activation(ell, ell, ACT.Ln, bias=1.0).then_inc(ell_made, 1)
                act.wait_ge(vt_done, j * 2 + a + 1)
                if a >= 1:
                    act.wait_ge(pva_done, j * 2 + a)
                act.activation(va, bank(2, 0, SEQ), ACT.Copy).then_inc(va_made, 1)
                act.wait_ge(spl_masked, j * 2 + a + 1)
                act.activation(spl_cut[0], spl, ACT.Copy).then_inc(spl_hi, 1)
                between[0]()
                act.wait_ge(stay_made, j * 2 + a + 1)
                act.activation(wts, arg, ACT.Exp).then_inc(wts_made, 1)
                between[1]()

            def attend_b(a, j, hh):
                h = j * 4 + (2 * a + hh)
                act.wait_ge(peak_made, h + 1)
                if 2 * a + hh >= 1:
                    act.wait_ge(inv_made, h)
                act.activation(prob[:, 0:W0], prob[:, 0:W0], ACT.Exp, bias=npeak[:, 0:1], accum_out=total[:, 0:1])
                act.activation(prob[:, W0:W0 + W1], prob[:, W0:W0 + W1], ACT.Exp, bias=npeak[:, 1:2],
                               accum_out=total[:, 1:2]).then_inc(prob_made, 1)

            def transposed_b(a, j, hh):
                h = j * 4 + (2 * a + hh)
                act.wait_ge(pt_done, h + 1)
                act.activation(prob[:, 0:W0], bank(5, 0, W0), ACT.Copy)
                act.activation(prob[:, W0:W0 + W1].rearrange("p (m n) -> p m n", m=2), banks(6, 2, W0), ACT.Copy
                               ).then_inc(pt_made, 1)

            def value_b(p, j, t):
                par = p % 2
                if t == 0:
                    act.wait_ge(job_done, j * 6 + 3 * p + 3 if p else 1)
                    if p >= 1:
                        act.wait_ge(pvb_done, j * 4 + 2 * p)
                else:
                    act.wait_ge(w_used, j * 12 + B0 + 6 * p + 6 if p else B0 + 2)
                if p == 0:
                    act.wait_ge(xrs_made, NT * 2 + t + 1)
                act.activation(vb[:, t, :], bank((par + 1 + t) % 2 if p else t, 0, NG * P), ACT.Copy,
                               scale=x_rs(2, t)).then_inc(vb_made, 1)

            def step_b(p, j):
                s = B0 + 6 * p
                jj = j * 2
                hi(s + 4, jj)
                attend_b(p - 1, j, 0)
                hi(s + 5, jj)
                hi(s + 6, jj)
                transposed_b(p - 1, j, 0)
                hi(s + 7, jj)
                attend_b(p - 1, j, 1)
                hi(s + 8, jj)
                transposed_b(p - 1, j, 1)
                hi(s + 9, jj)
                for t in range(NT):
                    value_b(p, j, t)

            def silu_of(l, s, i, j, t):
                if t == 0:
                    act.wait_ge(up0_done, j * 2 + l * STEPS + i + 1)
                else:
                    act.wait_ge(w_used, j * 6 + s + 2)
                if i >= 1:
                    act.wait_ge(hid_made, j * 4 + 2 * (l * STEPS + i - 1) + t + 1)
                act.activation(silu[:, t, :], bank(4 + t, 0, FC), ACT.Silu, scale=x_rs(2 * l + 1, t)
                               ).then_inc(silu_made, 1)

            def swiglu_step(l, s0, i, j, units):
                s = s0 + 3 * i - 1
                for n, u in enumerate(units):
                    if n < NT and i == 1:
                        silu_of(l, s, i, j, n)
                    hi(u, j)
                    if n < NT and i > 1:
                        silu_of(l, s, i, j, n)

            def swiglu(l, s0, last_units):
                for t in range(NT):
                    act.wait_ge(xrs_made, NT * (2 * l + 1) + t + 1)
                    silu_of(l, s0, 0, 0, t)
                    if t == 0:
                        hi(s0 + 4)
                swiglu_step(l, s0, 1, 0, range(s0 + 5, s0 + 8))
                with act.Fori(0, (STEPS - 3) // 2) as j:
                    for i in (2, 3):
                        swiglu_step(l, s0, i, j, range(s0 + 3 * i + 2, s0 + 3 * i + 5))
                swiglu_step(l, s0, STEPS - 1, 0, last_units)

            act.dma_start(gain_in[0:8 * KT, :], gain_rows).then_inc(gain_in_s, 16)
            act.dma_start(gain_in[8 * KT:9 * KT, :], g_kv.rearrange("(k p) -> k p", p=P)).then_inc(gain_in_s, 16)
            act.preload_act_table_set("natural_log_exp_and_others")
            act.wait_ge(gain_made, 1)
            cut_x(0, 0, 6, xt, 0)
            hi(A0)
            cut_x(0, 1, 4, xt, 0)
            hi(A0 + 1)
            for t in range(NT):
                act.wait_ge(x_in[t], 16)
                if t:
                    act.wait_ge(xsq_made, t)
                act.activation(squares_a, xn[:, t, :], ACT.Square, scale=D ** -0.5, accum_out=x_sq(0, t)
                               ).then_inc(xsq_made, 1)
            for u in range(2, 6):
                hi(A0 + u)
                if u == 3:
                    act.wait_ge(later_in, 16)
                    act.wait_ge(ones_in, 16)
                    act.activation(later_r, later, ACT.Copy)
                    act.activation(ones_r, ones[:, :], ACT.Copy).then_inc(exact_made, 1)

            def step_a(a, j):
                s = A0 + 3 * a + 6
                attend_a(a, j, [lambda: (hi(s, j), hi(s + 1, j)), lambda: hi(s + 2, j)])

            step_a(0, 0)
            act.preload_act_table_set("natural_log_exp_and_others")
            with act.Fori(0, 2) as j:
                step_a(1, j)
                step_a(2, j)
            step_a(PAIRS - 3, 0)
            attend_a(PAIRS - 2, 0, [lambda: (hi(WOA0), hi(WOA0 + 1)), lambda: None])
            attend_a(PAIRS - 1, 0, [lambda: (hi(WOA0 + 2), hi(WOA0 + 3)), lambda: (hi(FA0), hi(FA0 + 1))])
            boundary(0, WOA0 + 3, 2)
            swiglu(0, FA0, [B0 - 1, B0, B0 + 1])
            hi(B0 + 2)
            hi(B0 + 3)
            for t in range(NT):
                square_h(1, t, B0 - 1)
            cut_x(2, 0, 6, xkv, 8)
            square_x(1, 0)
            cut_x(2, 0, 6, xt, 4, 4 * KT)
            cut_x(2, 1, 4, xkv, 8)
            value_b(0, 0, 0)
            cut_x(2, 1, 4, xt, 4, 5 * KT)
            square_x(1, 1)
            value_b(0, 0, 1)
            act.preload_act_table(ACT.Exp)
            hi(B0 + 4)
            hi(B0 + 5)
            for u in range(6, 10):
                hi(B0 + u)
            with act.Fori(0, 3) as j:
                step_b(1, j)
                step_b(2, j)
            step_b(PAIRS - 1, 0)
            attend_b(PAIRS - 1, 0, 0)
            hi(FB0)
            transposed_b(PAIRS - 1, 0, 0)
            attend_b(PAIRS - 1, 0, 1)
            transposed_b(PAIRS - 1, 0, 1)
            hi(FB0 + 1)
            boundary(2, WOB0 + 3, 6)
            swiglu(1, FB0, [UNITS - 1])
            silu_of(1, UNITS - 4, STEPS - 1, 0, 1)
            for t in range(NT):
                square_h(3, t, UNITS - 1)

        @block.vector
        def _(dve):
            def lo(s, j=0):
                dve.wait_ge(hi_made, j * 6 + s + 1)
                n, c = size(s), s % CUT
                dve.tensor_tensor(w_lo[:, c, 0:n], raw[:, s % RAW, 0:n], w_hi[:, c, 0:n].bitcast(F32), ALU.subtract
                                  ).then_inc(lo_made, 1)

            def cut_x(n, t, first_bank, dst, gain, ks=range(KT)):
                for k in ks:
                    if k % 4 == 0:
                        dve.wait_ge(xt_hi, KT * n + k + 4)
                    dve.scalar_tensor_tensor(dst[:, 1, k, P * t:P * t + P], bank(first_bank + k // 4, P * (k % 4), P),
                                             gains[:, KT * gain + k:KT * gain + k + 1],
                                             dst[:, 0, k, P * t:P * t + P].bitcast(F32), ALU.mult, ALU.subtract
                                             ).then_inc(xt_made, 1)

            def scale_h(b, t, halves=range(2)):
                dve.wait_ge(post_in, 16 * (b + 1))
                for half in halves:
                    n, cols = 2 * (NT * b + t) + half + 1, slice(HALF * half, HALF * half + HALF)
                    if t:
                        dve.wait_ge(x_made, n - 2)
                    dve.wait_ge(hsq_made, n)
                    dve.tensor_tensor(delta[:, cols], bank(2 * t + half), post[:, cols], ALU.mult
                                      ).then_inc(delta_made, 1)

            def update(b, t, halves=range(2)):
                for half in halves:
                    n, cols = 2 * (NT * b + t) + half + 1, slice(HALF * half, HALF * half + HALF)
                    if half == 0:
                        dve.wait_ge(hrs_made, NT * b + t + 1)
                    dve.wait_ge(delta_made, n)
                    dve.scalar_tensor_tensor(xn[:, t, cols], delta[:, cols], h_rs(b, t), xn[:, t, cols],
                                             ALU.mult, ALU.add).then_inc(x_made, 1)

            def boundary(b, s, gain):
                n = 2 if b == 0 else 8
                scale_h(b, 0)
                update(b, 0)
                cut_x(n, 0, 6, xt, gain)
                scale_h(b, 1)
                update(b, 1)
                cut_x(n + 1, 1, 0, xt, gain)
                lo(s)

            def make_diagonal(n):
                dve.wait_ge(xrs_made, NT * n + NT)
                for t in range(NT):
                    inst = dve.tensor_scalar(ob[:, t, :], eye[:, :], x_rs(n, t), None, ALU.mult)
                inst.then_inc(diag_made, 1)

            def take_rows(use):
                dve.wait_ge(rows_done, use)
                dve.tensor_copy(rows[:, :], bank(2, 0, SEQ)).then_inc(rows_made, 1)
                dve.wait_ge(rows_made, use)

            def cut_ot(k, src, n):
                dve.tensor_copy(ot[:, 0, k, :], src).then_inc(ot_hi, 1)
                dve.wait_ge(ot_hi, n)
                dve.tensor_tensor(ot[:, 1, k, :], src, ot[:, 0, k, :].bitcast(F32), ALU.subtract).then_inc(ot_made, 1)

            def outputs_a(a, j):
                dve.wait_ge(pva_done, j * 2 + a + 1)
                cut_ot_at(j * 2 + a, bank(7, 0, SEQ), j * 2 + a + 1)

            def cut_ot_at(k, src, n):
                if isinstance(k, int):
                    cut_ot(k, src, n)
                    return
                src3 = src.rearrange("p (o n) -> p o n", o=1)
                dve.tensor_copy(ot[:, 0, ds(k, 1), :], src3).then_inc(ot_hi, 1)
                dve.wait_ge(ot_hi, n)
                dve.tensor_tensor(ot[:, 1, ds(k, 1), :], src3, ot[:, 0, ds(k, 1), :].bitcast(F32), ALU.subtract
                                  ).then_inc(ot_made, 1)

            def diagonals(buf):
                return buf.rearrange("p h (b n) -> p h b n", n=P)[:, :, 0:3:2, :]

            strict4 = strict.rearrange("p (h b n) -> p h b n", h=1, b=1).broadcast_to([P, 2, 2, P])

            def scores_a(a, j):
                z = banks(3, 2, WA)
                dve.wait_ge(ell_made, j * 2 + a + 1)
                dve.scalar_tensor_tensor(spl, z, 0.0, ell, ALU.max, ALU.add).then_inc(spl_made, 1)
                dve.wait_ge(spl_made, j * 2 + a + 1)
                dve.tensor_tensor(diagonals(spl), diagonals(spl), strict4, ALU.mult).then_inc(spl_masked, 1)
                dve.scalar_tensor_tensor(arg, z, 0.0, ell, ALU.min, ALU.subtract).then_inc(arg_made, 1)
                dve.wait_ge(spl_hi, j * 2 + a + 1)
                dve.tensor_tensor(spl_cut[1], spl, spl_cut[0].bitcast(F32), ALU.subtract).then_inc(spl_cut_made, 1)

            def stay_a(a, j):
                dve.wait_ge(arg_made, j * 2 + a + 1)
                dve.wait_ge(r_done, j * 2 + a + 1)
                for lo_, n, b in ((0, SEQ, 5), (SEQ, P, 6)):
                    part = arg[:, :, lo_:lo_ + n]
                    inst = dve.tensor_tensor(part, part, two_heads(b, n), ALU.subtract)
                inst.then_inc(stay_made, 1)

            def mask_a(a, j):
                dve.wait_ge(wts_made, j * 2 + a + 1)
                dve.tensor_tensor(diagonals(wts), diagonals(wts), strict4, ALU.mult).then_inc(wts_masked, 1)

            def take_qk_a(p, j):
                dve.wait_ge(w_used, j * 6 + A0 + 3 * p + 2)
                dve.scalar_tensor_tensor(qa, bank(0, 0, SEQ), SCALE, rows[:, :], ALU.mult, ALU.mult)
                dve.tensor_tensor(ka, bank(0, SEQ, SEQ), rows[:, :], ALU.mult).then_inc(qka_made, 1)

            def take_v_a(p, j):
                dve.wait_ge(w_used, j * 6 + A0 + 3 * p + 3)
                if p >= 1:
                    dve.wait_ge(vt_done, j * 2 + p)
                dve.tensor_tensor(va_t, bank(1, 0, SEQ), rows[:, :], ALU.mult).then_inc(vat_made, 1)

            def step_a(p, j):
                s = A0 + 3 * p + 3
                if p >= 2:
                    outputs_a(p - 2, j)
                scores_a(p - 1, j)
                take_qk_a(p, j)
                stay_a(p - 1, j)
                lo(s, j)
                mask_a(p - 1, j)
                take_v_a(p, j)
                lo(s + 1, j)
                lo(s + 2, j)

            rows2 = rows[:, :].rearrange("p (g n) -> p g n", g=1).broadcast_to([P, 2, SEQ])

            def two(b):
                return bank(b).rearrange("p (g n) -> p g n", g=2)

            def take_q01(p, j):
                par = p % 2
                dve.wait_ge(job_done, j * 6 + 3 * p + 1 if p else 2)
                dve.scalar_tensor_tensor(qb[:, par, 0:2, :], two(par), SCALE, rows2, ALU.mult, ALU.mult
                                         ).then_inc(qkb_made, 1)

            def take_q2k0(p, j):
                par = p % 2
                dve.wait_ge(job_done, j * 6 + 3 * p + 2 if p else 3)
                dve.scalar_tensor_tensor(qb[:, par, 2, :], bank(1 - par, 0, SEQ), SCALE, rows[:, :],
                                         ALU.mult, ALU.mult)
                dve.tensor_tensor(kb[:, par, 0, :], bank(1 - par, SEQ, SEQ), rows[:, :], ALU.mult
                                  ).then_inc(qkb_made, 1)

            def take_k12(p, j):
                par = p % 2
                dve.wait_ge(w_used, j * 12 + B0 + 6 * p + 4 if p else B0 + 6)
                dve.tensor_tensor(kb[:, par, 1:3, :], two(par), rows2, ALU.mult).then_inc(qkb_made, 1)

            def peaks(a, j, hh):
                h = j * 4 + (2 * a + hh)
                dve.wait_ge(bias_made, h + 1)
                if 2 * a + hh >= 1:
                    dve.wait_ge(pvb_done, h)
                dve.wait_ge(s_done, h + 1)
                dve.memset(npeak, 0.0)
                dve.tensor_tensor_reduce(
                    out=prob[:, 0:W0].rearrange("p (g n) -> p g n", g=NG),
                    in0=bank(2, 0, W0).rearrange("p (g n) -> p g n", g=NG), in1=bias[:, hh, :, P:2 * P],
                    scale=1.0, scalar=LOWEST, op0=ALU.add, op1=ALU.max, accum_out=peak[:, 0:1])
                dve.tensor_tensor_reduce(
                    out=prob[:, W0:W0 + W1].rearrange("p (g n) -> p g n", g=NG),
                    in0=ps[:, 3 * 512:3 * 512 + W1].rearrange("p (g n) -> p g n", g=NG), in1=bias[:, hh, :, :],
                    scale=1.0, scalar=LOWEST, op0=ALU.add, op1=ALU.max, accum_out=peak[:, 1:2]).then_inc(sum_made, 1)
                dve.wait_ge(sum_made, h + 1)
                dve.tensor_scalar(npeak, peak, -1.0, None, ALU.mult).then_inc(peak_made, 1)

            def invert(a, j, hh):
                dve.wait_ge(prob_made, j * 4 + (2 * a + hh) + 1)
                dve.reciprocal(inv, total).then_inc(inv_made, 1)

            def take_o(a, j, hh):
                h = j * 4 + (2 * a + hh)
                dve.wait_ge(inv_made, h + 1)
                if 2 * a + hh >= 2 and hh == 0:
                    dve.wait_ge(obt_done, j * 2 + a)
                dve.wait_ge(pvb_done, h + 1)
                for t in range(NT):
                    inst = dve.tensor_scalar(ob[:, t, DH * hh:DH * hh + DH], bank(5, DH * t, DH), inv[:, t:t + 1],
                                             None, ALU.mult)
                inst.then_inc(ob_made, 1)

            def outputs_b(a, j):
                dve.wait_ge(obt_done, j * 2 + a + 1)
                cut_ot_at(j * 2 + a, bank(6, 0, SEQ), j * 2 + (PAIRS + a + 1))

            def step_b(p, j):
                s, jj = B0 + 6 * p, j * 2
                peaks(p - 1, j, 0)
                lo(s + 4, jj)
                take_q01(p, j)
                lo(s + 5, jj)
                invert(p - 1, j, 0)
                take_q2k0(p, j)
                lo(s + 6, jj)
                take_o(p - 1, j, 0)
                peaks(p - 1, j, 1)
                take_k12(p, j)
                lo(s + 7, jj)
                invert(p - 1, j, 1)
                lo(s + 8, jj)
                take_o(p - 1, j, 1)
                lo(s + 9, jj)
                outputs_b(p - 1, j)

            def gated(l, i, j, t):
                n = l * STEPS + i
                dve.wait_ge(silu_made, j * 4 + 2 * n + t + 1)
                if i >= 1:
                    dve.wait_ge(ht_done, j * 2 + n)
                dve.scalar_tensor_tensor(hid[:, t, :], bank(4 + t, FC, FC), x_rs(2 * l + 1, t), silu[:, t, :],
                                         ALU.mult, ALU.mult).then_inc(hid_made, 1)

            def cut_hidden(l, i, j):
                n, k = l * STEPS + i, hidden_at(i)
                src = two(6)
                dve.wait_ge(ht_done, j * 2 + n + 1)
                dve.tensor_copy(ot[:, 0, k, :], src).then_inc(ht_hi, 1)
                dve.wait_ge(ht_hi, j * 2 + n + 1)
                dve.tensor_tensor(ot[:, 1, k, :], src, ot[:, 0, k, :].bitcast(F32), ALU.subtract
                                  ).then_inc(ht_made, 1)

            def swiglu_step(l, i, j, units):
                if i > 1:
                    lo(units[0], j)
                cut_hidden(l, i - 1, j)
                gated(l, i, j, 0)
                if i == 1:
                    lo(units[0])
                if len(units) > 1:
                    lo(units[1], j)
                gated(l, i, j, 1)
                if len(units) > 2:
                    lo(units[2], j)

            def swiglu(l, s0, last_units):
                gated(l, 0, 0, 0)
                lo(s0 + 3)
                gated(l, 0, 0, 1)
                lo(s0 + 4)
                swiglu_step(l, 1, 0, range(s0 + 5, s0 + 8))
                with dve.Fori(0, (STEPS - 3) // 2) as j:
                    for i in (2, 3):
                        swiglu_step(l, i, j, range(s0 + 3 * i + 2, s0 + 3 * i + 5))
                swiglu_step(l, STEPS - 1, 0, last_units)

            dve.memset(rows[:, :], 0.0).then_inc(zeros_made, 1)
            dve.wait_ge(gain_done, 1)
            dve.tensor_copy(gains[:, :], bank(3, 0, 9 * KT)).then_inc(gain_made, 1)
            dve.wait_ge(gain_made, 1)
            cut_x(0, 0, 6, xt, 0)
            lo(A0)
            cut_x(1, 1, 4, xt, 0)
            lo(A0 + 1)
            lo(A0 + 2)
            make_diagonal(0)
            lo(A0 + 3)
            take_rows(1)
            take_qk_a(0, 0)
            dve.wait_ge(bias_done, 1)
            dve.tensor_copy(bias_out[0:NH, :], ps[0:NH, 3 * 512:3 * 512 + 3 * P]).then_inc(bias_out_made, 1)
            lo(A0 + 4)
            take_v_a(0, 0)
            lo(A0 + 5)
            dve.wait_ge(mask_in_s, 16)
            dve.tensor_copy(mask_b[:, :, :], mask_in).then_inc(mask_made, 1)
            dve.wait_ge(strict_in, 16)
            step_a(1, 0)
            step_a(2, 0)
            with dve.Fori(0, 2) as j:
                step_a(3, j)
                step_a(4, j)
            outputs_a(PAIRS - 3, 0)
            scores_a(PAIRS - 2, 0)
            take_qk_a(PAIRS - 1, 0)
            lo(WOA0)
            take_v_a(PAIRS - 1, 0)
            stay_a(PAIRS - 2, 0)
            lo(WOA0 + 1)
            mask_a(PAIRS - 2, 0)
            scores_a(PAIRS - 1, 0)
            outputs_a(PAIRS - 2, 0)
            lo(WOA0 + 2)
            stay_a(PAIRS - 1, 0)
            lo(WOA0 + 3)
            mask_a(PAIRS - 1, 0)
            outputs_a(PAIRS - 1, 0)
            lo(FA0)
            lo(FA0 + 1)
            boundary(0, FA0 + 2, 2)
            swiglu(0, FA0, [B0 - 1, B0])
            cut_hidden(0, STEPS - 1, 0)
            for u in range(1, 4):
                lo(B0 + u)
            scale_h(1, 0)
            update(1, 0)
            scale_h(1, 1, [0])
            cut_x(4, 0, 6, xkv, 8, range(4))
            scale_h(1, 1, [1])
            update(1, 1, [0])
            cut_x(4, 0, 6, xkv, 8, range(4, 8))
            update(1, 1, [1])
            cut_x(6, 1, 4, xkv, 8)
            cut_x(5, 0, 6, xt, 4)
            cut_x(7, 1, 4, xt, 4)
            make_diagonal(2)
            lo(B0 + 4)
            lo(B0 + 5)
            take_rows(2)
            take_q01(0, 0)
            lo(B0 + 6)
            take_q2k0(0, 0)
            lo(B0 + 7)
            lo(B0 + 8)
            take_k12(0, 0)
            lo(B0 + 9)
            step_b(1, 0)
            step_b(2, 0)
            with dve.Fori(0, 2) as j:
                step_b(3, j)
                step_b(4, j)
            step_b(PAIRS - 1, 0)
            peaks(PAIRS - 1, 0, 0)
            lo(FB0)
            invert(PAIRS - 1, 0, 0)
            take_o(PAIRS - 1, 0, 0)
            peaks(PAIRS - 1, 0, 1)
            invert(PAIRS - 1, 0, 1)
            take_o(PAIRS - 1, 0, 1)
            outputs_b(PAIRS - 1, 0)
            lo(FB0 + 1)
            boundary(2, FB0 + 2, 6)
            swiglu(1, FB0, [UNITS - 1])
            cut_hidden(1, STEPS - 1, 0)
            for t in range(NT):
                scale_h(3, t)
                update(3, t)

        @block.tensor
        def _(pe):
            mm = nc.tensor.matmul

            def by_x(out, xs, ws, start, stop):
                mm(out, xs[0], ws[0], start=start, stop=False)
                mm(out, xs[0], ws[1], start=False, stop=False)
                return mm(out, xs[1], ws[0], start=False, stop=stop)

            def by_w(out, ws, xs, start, stop):
                mm(out, ws[0], xs[0], start=start, stop=False)
                mm(out, ws[0], xs[1], start=False, stop=False)
                return mm(out, ws[1], xs[0], start=False, stop=stop)

            def cut_unit(s, **dims):
                n = size(s)
                spec = "p (k g n) -> p k g n" if "g" in dims else "p (k n) -> p k n"
                return [w[:, s % CUT, 0:n].rearrange(spec, **dims) for w in (w_hi, w_lo)]

            def transpose_x(n, t, first_bank, halves=range(2)):
                for half in halves:
                    if n:
                        pe.wait_ge(x_made, 2 * (NT * (n - 1) + t) + half + 1)
                    for k in range(4 * half, 4 * half + 4):
                        inst = pe.transpose(bank(first_bank + half, P * (k % 4), P), xn[:, t, P * k:P * k + P],
                                            eye[:, :])
                    inst.then_inc(xt_done, 1)

            def spread_rows(use):
                pe.wait_ge(diag_made, use)
                for t in range(NT):
                    inst = mm(bank(2, P * t, P), ones[:, :], ob[:, t, :], start=True, stop=True)
                inst.then_inc(rows_done, 1)

            def project_a(p, j, c, b, col, ks=range(KT)):
                s = A0 + 3 * p + c
                pe.wait_ge(lo_made, j * 6 + s + 1)
                w = cut_unit(s, k=KT)
                for k in ks:
                    if p == 0 and c == 0:
                        pe.wait_ge(xt_made, KT + k + 1)
                    inst = by_w(bank(b, col, SEQ), [v[:, k, :] for v in w], [xt[:, n, k, :] for n in range(2)],
                                k == 0, k == KT - 1)
                if k == KT - 1:
                    inst.then_inc(w_used, 1)

            def scores_a(a, j):
                pe.wait_ge(qka_made, j * 2 + a + 1)
                if a >= 1:
                    pe.wait_ge(arg_made, j * 2 + a)
                for hh in range(2):
                    rows_ = slice(DH * hh, DH * hh + DH)
                    mm(bank(3 + hh, 0, SEQ), ka[rows_, 0:P], qa[rows_, :], start=True, stop=True)
                    inst = mm(bank(3 + hh, SEQ, P), ka[rows_, P:SEQ], qa[rows_, P:SEQ], start=True, stop=True)
                inst.then_inc(z_done, 1)

            def turn_v(a, j):
                pe.wait_ge(vat_made, j * 2 + a + 1)
                if a >= 1:
                    pe.wait_ge(va_made, j * 2 + a)
                for t in range(NT):
                    inst = pe.transpose(bank(2, P * t, P), va_t[:, P * t:P * t + P], eye[:, :])
                inst.then_inc(vt_done, 1)

            def sums_a(a, j):
                pe.wait_ge(spl_cut_made, j * 2 + a + 1)
                if a >= 1:
                    pe.wait_ge(stay_made, j * 2 + a)
                for out_, w, cols in ((two_heads(5, SEQ), later_r, slice(0, SEQ)),
                                      (two_heads(5, SEQ)[:, :, P:SEQ], ones_r, slice(SEQ, WA)),
                                      (two_heads(6, P), later_r, slice(SEQ, WA))):
                    for n in range(2):
                        inst = mm(out_, w, spl_cut[n][:, :, cols], start=w is later_r and n == 0,
                                  stop=n == 1 and cols.stop == WA, skip_group_check=True)
                inst.then_inc(r_done, 1)

            def outputs_a(a, j):
                pe.wait_ge(va_made, j * 2 + a + 1)
                if a >= 1:
                    pe.wait_ge(ot_made, j * 2 + a)
                pe.wait_ge(wts_masked, j * 2 + a + 1)
                for hh in range(2):
                    out = ps[DH * hh:DH * hh + DH, 7 * 512:7 * 512 + SEQ]
                    mm(out, va[:, DH * hh:DH * hh + DH], wts[:, hh, 0:SEQ], start=True, stop=False,
                       skip_group_check=True)
                    inst = mm(out[:, P:SEQ], va[:, P + DH * hh:P + DH * hh + DH], wts[:, hh, SEQ:WA],
                              start=False, stop=True, skip_group_check=True)
                inst.then_inc(pva_done, 1)

            def step_a(p, j):
                scores_a(p - 1, j)
                if p >= 2:
                    outputs_a(p - 2, j)
                turn_v(p - 1, j)
                project_a(p, j, 0, 0, 0)
                project_a(p, j, 1, 0, SEQ)
                project_a(p, j, 2, 1, 0, range(2))
                sums_a(p - 1, j)
                project_a(p, j, 2, 1, 0, range(2, KT))

            def out_proj(s0, n0, t, ks):
                for k in ks:
                    s = s0 + k // 2
                    pe.wait_ge(lo_made, s + 1)
                    pe.wait_ge(ot_made, n0 + k + 1)
                    w = cut_unit(s, k=2)
                    for half in range(2):
                        inst = by_x(bank(2 * t + half), [ot[:, n, k, P * t:P * t + P] for n in range(2)],
                                    [v[:, k % 2, HALF * half:HALF * half + HALF] for v in w], k == 0, k == KT - 1)
                        if k == KT - 1 and half == 1 - t:
                            inst.then_inc(acc_done, 1)
                    if t == 1 and k % 2:
                        inst.then_inc(w_used, 1)

            def up(l, s, i, j, t, ks=range(KT)):
                if i >= 1:
                    pe.wait_ge(hid_made, j * 4 + 2 * (l * STEPS + i - 1) + t + 1)
                for k in ks:
                    if k % 4 == 0:
                        pe.wait_ge(lo_made, j * 6 + s + k // 4 + 1)
                    w = cut_unit(s + k // 4, k=4)
                    if i == 0:
                        pe.wait_ge(xt_made, (2 + 6 * l) * KT + KT * t + k + 1)
                    inst = by_x(bank(4 + t), [xt[:, n, k, P * t:P * t + P] for n in range(2)],
                                [v[:, k % 4, :] for v in w], k == 0, k == KT - 1)
                    if t == 1 and k % 4 == 3:
                        inst.then_inc(w_used, 1)
                if t == 0 and k == KT - 1:
                    inst.then_inc(up0_done, 1)

            def transpose_hidden(l, i, j):
                n = l * STEPS + i
                pe.wait_ge(hid_made, j * 4 + 2 * n + 2)
                if n >= 1:
                    pe.wait_ge(ht_made, j * 2 + n)
                for f in range(2):
                    for t in range(NT):
                        inst = pe.transpose(bank(6, SEQ * f + P * t, P), hid[:, t, P * f:P * f + P], eye[:, :])
                inst.then_inc(ht_done, 1)

            def down_part(l, s, i, j, t, parts_):
                pe.wait_ge(lo_made, j * 6 + s + 1)
                pe.wait_ge(ht_made, j * 2 + l * STEPS + i + 1)
                w = cut_unit(s, k=2)
                for f, half in parts_:
                    inst = by_x(bank(2 * t + half),
                                [ot[:, n, hidden_at(i).start + f, P * t:P * t + P] for n in range(2)],
                                [v[:, f, HALF * half:HALF * half + HALF] for v in w],
                                i == 0 and f == 0, i == STEPS - 1 and f == 1)
                return inst

            FH = [(f, half) for f in range(2) for half in range(2)]

            def down(l, s, i, j):
                down_part(l, s, i, j, 0, FH)
                down_part(l, s, i, j, 1, FH).then_inc(w_used, 1)

            def last_steps(l, s0):
                last = STEPS - 1
                s = s0 + 3 * last - 1
                up(l, s, last, 0, 0)
                transpose_hidden(l, last - 1, 0)
                up(l, s, last, 0, 1)
                down_part(l, s + 2, last - 1, 0, 0, FH[:2])
                transpose_hidden(l, last, 0)
                down_part(l, s + 2, last - 1, 0, 0, FH[2:])
                down_part(l, s + 2, last - 1, 0, 1, FH[:2])
                down_part(l, s + 3, last, 0, 0, FH).then_inc(acc_done, 1)
                down_part(l, s + 2, last - 1, 0, 1, FH[2:]).then_inc(w_used, 1)
                down_part(l, s + 3, last, 0, 1, [(0, 0), (1, 0)]).then_inc(acc_done, 1)
                down_part(l, s + 3, last, 0, 1, [(0, 1), (1, 1)]).then_inc(w_used, 1)

            def swiglu_step(l, s0, i, j):
                s = s0 + 3 * i - 1
                up(l, s, i, j, 0)
                transpose_hidden(l, i - 1, j)
                up(l, s, i, j, 1)
                down(l, s + 2, i - 1, j)

            def swiglu(l, s0, b):
                up(l, s0, 0, 0, 0, range(5))
                transpose_x(b + 1, 1, 0, [0])
                up(l, s0, 0, 0, 0, [5, 6])
                transpose_x(b + 1, 1, 0, [1])
                up(l, s0, 0, 0, 0, [7])
                up(l, s0, 0, 0, 1)
                swiglu_step(l, s0, 1, 0)
                with pe.Fori(0, (STEPS - 3) // 2) as j:
                    swiglu_step(l, s0, 2, j)
                    swiglu_step(l, s0, 3, j)
                last_steps(l, s0)

            def columns_b(p, jj, c, g, b, col):
                x_ = xt if c == 0 else xkv
                for k in range(KT):
                    s = B0 + 6 * p + 2 * (c if p else c + 1) + k // 4
                    if k % 4 == 0:
                        pe.wait_ge(lo_made, jj * 6 + s + 1)
                        w = cut_unit(s, k=4, g=NG)
                    if p == 0 and c == 0 and g == 0:
                        pe.wait_ge(xt_made, 7 * KT + k + 1)
                    inst = by_w(bank(b, col, SEQ), [v[:, k % 4, g, :] for v in w], [x_[:, n, k, :] for n in range(2)],
                                k == 0, k == KT - 1)
                    if g == NG - 1 and k % 4 == 3:
                        inst.then_inc(w_used, 1)
                return inst

            def values_b(p, jj, t, ks=range(KT)):
                for k in ks:
                    s = B0 + 6 * p + (4 if p else 0) + k // 4
                    if k % 4 == 0:
                        pe.wait_ge(lo_made, jj * 6 + s + 1)
                    w = cut_unit(s, k=4)
                    if p == 0:
                        pe.wait_ge(xt_made, (4 + t) * KT + k + 1)
                    inst = by_x(bank((p + 1 + t) % 2 if p else t, 0, NG * P),
                                [xkv[:, n, k, P * t:P * t + P] for n in range(2)], [v[:, k % 4, :] for v in w], k == 0, k == KT - 1)
                    if t == 1 and k % 4 == 3:
                        inst.then_inc(w_used, 1)
                if t == 0 and k == KT - 1:
                    inst.then_inc(job_done, 1)

            def scores_b(a, j, hh):
                par, r = a % 2, slice(DH * hh, DH * hh + DH)
                pe.wait_ge(qkb_made, j * 6 + 3 * a + 3)
                if 2 * a + hh >= 1:
                    pe.wait_ge(sum_made, j * 4 + 2 * a + hh)
                for g in range(NG):
                    mm(bank(2, P * g, P), qb[r, par, g, 0:P], kb[r, par, g, 0:P], start=True, stop=True)
                for g in range(NG):
                    inst = mm(ps[:, 3 * 512 + SEQ * g:3 * 512 + SEQ * g + SEQ], qb[r, par, g, P:SEQ],
                              kb[r, par, g, :], start=True, stop=True)
                inst.then_inc(s_done, 1)

            def transpose_b(a, j, hh):
                h = j * 4 + (2 * a + hh)
                pe.wait_ge(prob_made, h + 1)
                if 2 * a + hh >= 1:
                    pe.wait_ge(ob_made, h)
                if a >= 1 and hh == 0:
                    pe.wait_ge(ot_made, j * 2 + PAIRS + a)
                for n in range(3 * NG):
                    inst = pe.transpose(bank(5 + n // 3, P * (n % 3), P), prob[:, P * n:P * n + P], eye[:, :])
                inst.then_inc(pt_done, 1)

            def outputs_b(a, j, hh):
                h = j * 4 + (2 * a + hh)
                pe.wait_ge(vb_made, j * 4 + 2 * a + 2)
                pe.wait_ge(pt_made, h + 1)
                for t in range(NT):
                    blocks = [(g, kt) for g in range(NG) for kt in range(t + 1)]
                    for n, (g, kt) in enumerate(blocks):
                        at_ = W0 * t + P * n
                        inst = mm(bank(5, DH * t, DH), prob[:, at_:at_ + P],
                                  vb[:, kt, P * g + DH * hh:P * g + DH * hh + DH],
                                  start=n == 0, stop=n == len(blocks) - 1)
                inst.then_inc(pvb_done, 1)

            def turn_b(a, j):
                pe.wait_ge(ob_made, j * 4 + 2 * a + 2)
                for t in range(NT):
                    inst = pe.transpose(bank(6, P * t, P), ob[:, t, :], eye[:, :])
                inst.then_inc(obt_done, 1)

            def step_b(p, j):
                jj, par, a = j * 2, p % 2, p - 1
                scores_b(a, j, 0)
                pe.wait_ge(vb_made, j * 4 + 2 * p)
                columns_b(p, jj, 0, 0, par, 0)
                columns_b(p, jj, 0, 1, par, SEQ).then_inc(job_done, 1)
                transpose_b(a, j, 0)
                columns_b(p, jj, 0, 2, 1 - par, 0)
                columns_b(p, jj, 1, 0, 1 - par, SEQ).then_inc(job_done, 1)
                outputs_b(a, j, 0)
                scores_b(a, j, 1)
                pe.wait_ge(qkb_made, j * 6 + 3 * p + 1)
                columns_b(p, jj, 1, 1, par, 0)
                columns_b(p, jj, 1, 2, par, SEQ)
                transpose_b(a, j, 1)
                pe.wait_ge(qkb_made, j * 6 + 3 * p + 2)
                values_b(p, jj, 0)
                outputs_b(a, j, 1)
                pe.wait_ge(qkb_made, j * 6 + 3 * p + 3)
                values_b(p, jj, 1)
                turn_b(a, j)

            def keep_busy(n):
                for _ in range(n):
                    mm(bank(2, 0, SEQ), rows[:, 0:P], rows[:, :], start=True, stop=True)

            pe.wait_ge(zeros_made, 1)
            keep_busy(5)
            pe.wait_ge(eye_in, 16)
            pe.wait_ge(gain_in_s, 16 * 2)
            pe.transpose(bank(3, 0, 9 * KT), gain_in[0:9 * KT, :], eye[0:9 * KT, 0:9 * KT]).then_inc(gain_done, 1)
            for t in range(NT):
                pe.wait_ge(x_in[t], 16)
                transpose_x(0, t, 6 - 2 * t)
            keep_busy(7)
            project_a(0, 0, 0, 0, 0)
            project_a(0, 0, 1, 0, SEQ)
            pe.wait_ge(ones_in, 16)
            spread_rows(1)
            pe.wait_ge(bias_in, 32)
            pe.wait_ge(gain_made, 1)
            mm(ps[0:NH, 3 * 512:3 * 512 + 3 * P], rel_in[0:BUCKETS, :], select_in[0:BUCKETS, :],
               start=True, stop=True).then_inc(bias_done, 1)
            project_a(0, 0, 2, 1, 0)
            pe.wait_ge(bias_out_made, 1)
            pe.wait_ge(exact_made, 1)
            step_a(1, 0)
            step_a(2, 0)
            with pe.Fori(0, 2) as j:
                step_a(3, j)
                step_a(4, j)
            last = PAIRS - 1
            scores_a(last - 1, 0)
            outputs_a(last - 2, 0)
            turn_v(last - 1, 0)
            project_a(last, 0, 0, 0, 0)
            project_a(last, 0, 1, 0, SEQ)
            project_a(last, 0, 2, 1, 0)
            sums_a(last - 1, 0)
            scores_a(last, 0)
            turn_v(last, 0)
            out_proj(WOA0, 0, 0, [0, 1])
            outputs_a(last - 1, 0)
            out_proj(WOA0, 0, 0, [2, 3])
            sums_a(last, 0)
            pe.wait_ge(va_made, PAIRS)
            out_proj(WOA0, 0, 1, [0, 1])
            out_proj(WOA0, 0, 0, [4, 5, 6])
            outputs_a(last, 0)
            out_proj(WOA0, 0, 1, [2])
            out_proj(WOA0, 0, 0, [7])
            out_proj(WOA0, 0, 1, [3, 4, 5, 6])
            transpose_x(1, 0, 6, [0])
            out_proj(WOA0, 0, 1, [7])
            transpose_x(1, 0, 6, [1])
            swiglu(0, FA0, 0)
            transpose_x(2, 0, 6)
            values_b(0, 0, 0, range(6))
            transpose_x(2, 1, 4, [0])
            values_b(0, 0, 0, [6, 7])
            transpose_x(2, 1, 4, [1])
            values_b(0, 0, 1)
            pe.wait_ge(vb_made, 1)
            columns_b(0, 0, 0, 0, 0, 0)
            columns_b(0, 0, 0, 1, 0, SEQ).then_inc(job_done, 1)
            spread_rows(2)
            pe.wait_ge(vb_made, 2)
            columns_b(0, 0, 0, 2, 1, 0)
            columns_b(0, 0, 1, 0, 1, SEQ).then_inc(job_done, 1)
            pe.wait_ge(qkb_made, 1)
            columns_b(0, 0, 1, 1, 0, 0)
            columns_b(0, 0, 1, 2, 0, SEQ)
            with pe.Fori(0, 3) as j:
                step_b(1, j)
                step_b(2, j)
            step_b(PAIRS - 1, 0)
            scores_b(PAIRS - 1, 0, 0)
            pe.wait_ge(vb_made, 2 * PAIRS)
            out_proj(WOB0, PAIRS, 0, [0, 1, 2])
            transpose_b(PAIRS - 1, 0, 0)
            out_proj(WOB0, PAIRS, 0, [3])
            outputs_b(PAIRS - 1, 0, 0)
            scores_b(PAIRS - 1, 0, 1)
            out_proj(WOB0, PAIRS, 0, [4, 5, 6])
            transpose_b(PAIRS - 1, 0, 1)
            out_proj(WOB0, PAIRS, 1, [0])
            outputs_b(PAIRS - 1, 0, 1)
            out_proj(WOB0, PAIRS, 1, [1])
            turn_b(PAIRS - 1, 0)
            out_proj(WOB0, PAIRS, 1, [2])
            out_proj(WOB0, PAIRS, 0, [7])
            out_proj(WOB0, PAIRS, 1, range(3, 6))
            transpose_x(3, 0, 6, [0])
            out_proj(WOB0, PAIRS, 1, [6])
            transpose_x(3, 0, 6, [1])
            out_proj(WOB0, PAIRS, 1, [7])
            swiglu(1, FB0, 2)


NAMES = ["x", "norm_gains", "w_qkv_a", "w_o_a", "g_kv", "w_kv_b", "w_q_b", "w_o_b", "rel_bias", "w_gate_up", "w_down"]


def kernel(**inputs):
    import concourse.bacc as bacc
    from concourse.bass_utils import run_bass_kernel_spmd

    nc = bacc.Bacc("TRN2", target_bir_lowering=False, num_devices=1)
    arrays, args = {}, []
    for name, a in [(n, inputs[n]) for n in NAMES] + list(shape_constants().items()):
        a = np.ascontiguousarray(a)
        arrays[f"in_{name}"] = a
        args.append(nc.dram_tensor(f"in_{name}", a.shape, mybir.dt.from_np(a.dtype), kind="ExternalInput").ap())
    args.append(nc.dram_tensor("out_x", (1, SEQ, D), mybir.dt.float32, kind="ExternalOutput").ap())
    build(nc, *args)
    return run_bass_kernel_spmd(nc, [arrays], core_ids=[0]).results[0]["out_x"]
```
